# Optimizing a Trainium2 kernel written in Bass

```python
import jax, jax.numpy as jnp
from jax import lax
import numpy as np

D_MODEL = 1024
BATCH = 1
SEQ = 2048
DEPTH = 1
DEC_BATCH = 8
DEC_SEQ = 1
PAST_LEN = 16384
PAGE_SIZE = 128

N_HEADS = 8
N_KV_HEADS = 2
HEAD_DIM = 64
Q_GROUP = N_HEADS // N_KV_HEADS
ATTN_DIM = N_HEADS * HEAD_DIM
KV_DIM = N_KV_HEADS * HEAD_DIM
WINDOW = 128
ATTN_BLOCK = WINDOW
ROPE_THETA = 10000.0
ATTN_SCALE = HEAD_DIM ** -0.5
CONV_CH = D_MODEL - ATTN_DIM
CONV_WIDTH = 31
MIX_DIM = ATTN_DIM + CONV_CH
IN_DIM = ATTN_DIM + 2 * KV_DIM + 2 * CONV_CH
N_GROUPS = 4
EXPERTS_PER_GROUP = 8
N_EXPERTS = N_GROUPS * EXPERTS_PER_GROUP
TOP_K_IN_GROUP = 2
D_FF_EXPERT = 256
DISPATCH_BLOCK = 128
LN_EPS = 1e-5
NEG_INF = -1e30
ALPHA = (2.0 * DEPTH) ** 0.25
BETA = (8.0 * DEPTH) ** -0.25

kernel_name = "hymba_swa_sink_conformer_hiermoe_step"

def layer_norm(x, g, b):
    xf = x.astype(jnp.float32)
    mu = jnp.mean(xf, axis=-1, keepdims=True)
    var = jnp.mean(jnp.square(xf - mu), axis=-1, keepdims=True)
    y = (xf - mu) * lax.rsqrt(var + LN_EPS) * g.astype(jnp.float32) + b.astype(jnp.float32)
    return y.astype(x.dtype)

def rope(x, pos):
    half = HEAD_DIM // 2
    inv = ROPE_THETA ** (-jnp.arange(half, dtype=jnp.float32) / half)
    ang = pos.astype(jnp.float32)[:, None] * inv
    cos = jnp.cos(ang)[:, None, :]
    sin = jnp.sin(ang)[:, None, :]
    x1 = x[..., :half].astype(jnp.float32)
    x2 = x[..., half:].astype(jnp.float32)
    return jnp.concatenate([x1 * cos - x2 * sin, x2 * cos + x1 * sin], axis=-1).astype(x.dtype)

def window_mask(qpos, kpos):
    d = qpos[..., :, None] - kpos[..., None, :]
    return (d >= 0) & (d < WINDOW) & (kpos[..., None, :] >= 0)

def attend(q, k, v, mask, sinks):
    s = jnp.einsum('...qkgd,...skd->...kgqs', q, k).astype(jnp.float32) * ATTN_SCALE
    s = jnp.where(mask, s, NEG_INF)
    sink = jnp.broadcast_to(sinks.astype(jnp.float32).reshape(N_KV_HEADS, Q_GROUP, 1, 1), s.shape[:-1] + (1,))
    p = jax.nn.softmax(jnp.concatenate([s, sink], axis=-1), axis=-1)[..., :-1]
    return jnp.einsum('...kgqs,...skd->...qkgd', p.astype(v.dtype), v)

def banded_window_attention(q, k, v, sinks):
    b, t = q.shape[0], q.shape[1]
    nblk = t // ATTN_BLOCK
    qb = q.reshape(b, nblk, ATTN_BLOCK, N_KV_HEADS, Q_GROUP, HEAD_DIM)

    def band(z):
        zp = jnp.pad(z, ((0, 0), (ATTN_BLOCK, 0), (0, 0), (0, 0)))
        zp = zp.reshape(b, nblk + 1, ATTN_BLOCK, N_KV_HEADS, HEAD_DIM)
        return jnp.concatenate([zp[:, :-1], zp[:, 1:]], axis=2)

    qpos = jnp.arange(t).reshape(nblk, ATTN_BLOCK)
    kp_all = jnp.arange(-ATTN_BLOCK, t).reshape(nblk + 1, ATTN_BLOCK)
    kpos = jnp.concatenate([kp_all[:-1], kp_all[1:]], axis=-1)
    mask = window_mask(qpos, kpos)
    out = attend(qb, band(k), band(v), mask[:, None, None], sinks)
    return out.reshape(b, t, ATTN_DIM)

def cached_window_attention(q, keys, vals, pos, sinks):
    b, t = q.shape[0], q.shape[1]
    kpos = pos[0] - WINDOW + jnp.arange(WINDOW + t)
    mask = window_mask(pos, kpos)
    out = attend(q, keys, vals, mask[None, None, None], sinks)
    return out.reshape(b, t, ATTN_DIM)

def depthwise_causal_conv(u_ext, w, bias):
    y = lax.conv_general_dilated(u_ext, w[:, None, :].astype(u_ext.dtype), window_strides=(1,),
                                 padding='VALID', dimension_numbers=('NWC', 'WIO', 'NWC'),
                                 feature_group_count=CONV_CH)
    return y + bias

def hier_moe(x2d, w_rg, w_re, w1, w3, w2):
    n = x2d.shape[0]
    lg = jnp.einsum('nd,dg->ng', x2d, w_rg).astype(jnp.float32)
    p_group = jax.nn.softmax(lg, axis=-1)
    g_idx = jnp.argmax(lg, axis=-1)
    p_g = jnp.take_along_axis(p_group, g_idx[:, None], axis=-1)[:, 0]
    le = jnp.einsum('nd,dge->nge', x2d, w_re).astype(jnp.float32)
    le_sel = jnp.take_along_axis(le, g_idx[:, None, None], axis=1)[:, 0]
    top_v, top_i = lax.top_k(le_sel, TOP_K_IN_GROUP)
    gate = p_g[:, None] * jax.nn.softmax(top_v, axis=-1)
    expert = g_idx[:, None] * EXPERTS_PER_GROUP + top_i

    nk = n * TOP_K_IN_GROUP
    e_flat = expert.reshape(-1)
    tok = jnp.arange(nk) // TOP_K_IN_GROUP
    counts = jnp.zeros((N_EXPERTS,), jnp.int32).at[e_flat].add(1)
    padded = (counts + DISPATCH_BLOCK - 1) // DISPATCH_BLOCK * DISPATCH_BLOCK
    pad_end = jnp.cumsum(padded)
    pad_start = pad_end - padded
    start = jnp.cumsum(counts) - counts
    order = jnp.argsort(e_flat, stable=True)
    e_sorted = e_flat[order]
    dest_sorted = pad_start[e_sorted] + (jnp.arange(nk) - start[e_sorted])
    dest = jnp.zeros((nk,), jnp.int32).at[order].set(dest_sorted.astype(jnp.int32))
    n_blocks = (nk + DISPATCH_BLOCK - 1) // DISPATCH_BLOCK + N_EXPERTS
    xbuf = jnp.zeros((n_blocks * DISPATCH_BLOCK, x2d.shape[1]), x2d.dtype).at[dest].set(x2d[tok])
    block_expert = jnp.clip(jnp.searchsorted(pad_end, jnp.arange(n_blocks) * DISPATCH_BLOCK, side='right'),
                            0, N_EXPERTS - 1)

    def run_block(args):
        xb, e = args
        h = jax.nn.silu(xb @ w1[e]) * (xb @ w3[e])
        return h @ w2[e]

    ybuf = lax.map(run_block, (xbuf.reshape(n_blocks, DISPATCH_BLOCK, -1), block_expert))
    y = ybuf.reshape(n_blocks * DISPATCH_BLOCK, -1)[dest].reshape(n, TOP_K_IN_GROUP, -1)
    return jnp.einsum('nk,nkd->nd', gate.astype(x2d.dtype), y)

def decoder_layer(x, pos, prev_k, prev_v, conv_prefix, w_in, b_in, sinks, conv_w, conv_b,
                  ln_conv_g, ln_conv_b, w_out, b_out, ln1_g, ln1_b, w_rg, w_re, w1, w3, w2,
                  ln2_g, ln2_b):
    nb, t, _ = x.shape
    proj = jnp.einsum('btd,de->bte', x, w_in) + b_in
    q, k, v, ca, cg = jnp.split(proj, [ATTN_DIM, ATTN_DIM + KV_DIM, ATTN_DIM + 2 * KV_DIM,
                                       ATTN_DIM + 2 * KV_DIM + CONV_CH], axis=-1)
    q = rope(q.reshape(nb, t, N_HEADS, HEAD_DIM), pos).reshape(nb, t, N_KV_HEADS, Q_GROUP, HEAD_DIM)
    k = rope(k.reshape(nb, t, N_KV_HEADS, HEAD_DIM), pos)
    v = v.reshape(nb, t, N_KV_HEADS, HEAD_DIM)
    if prev_k is None:
        attn = banded_window_attention(q, k, v, sinks)
        keys, vals = k, v
    else:
        keys = jnp.concatenate([prev_k, k], axis=1)
        vals = jnp.concatenate([prev_v, v], axis=1)
        attn = cached_window_attention(q, keys, vals, pos, sinks)
    new_k = keys[:, -WINDOW:]
    new_v = vals[:, -WINDOW:]

    u = ca * jax.nn.sigmoid(cg)
    u_ext = jnp.concatenate([conv_prefix, u], axis=1)
    conv = jax.nn.silu(layer_norm(depthwise_causal_conv(u_ext, conv_w, conv_b), ln_conv_g, ln_conv_b))
    new_conv = u_ext[:, -(CONV_WIDTH - 1):]

    mix = jnp.einsum('bte,ed->btd', jnp.concatenate([attn, conv], axis=-1), w_out) + b_out
    h = layer_norm(ALPHA * x + mix, ln1_g, ln1_b)
    f = hier_moe(h.reshape(nb * t, D_MODEL), w_rg, w_re, w1, w3, w2).reshape(nb, t, D_MODEL)
    y = layer_norm(ALPHA * h + f, ln2_g, ln2_b)
    return y, new_k, new_v, new_conv

def setup_inputs(seed: int = 0) -> dict:
    key = jax.random.key(seed)
    ks = jax.random.split(key, 24)

    def nrm(k, shape, scale):
        return jax.random.normal(k, shape, jnp.float32) * scale

    col_scale = jnp.ones((IN_DIM,), jnp.float32).at[ATTN_DIM + KV_DIM:ATTN_DIM + 2 * KV_DIM].set(BETA)
    return {
        "x_prompt": nrm(ks[0], (BATCH, SEQ, D_MODEL), 1.0),
        "x_sample": nrm(ks[1], (DEC_BATCH, DEC_SEQ, D_MODEL), 1.0),
        "cache_k": nrm(ks[2], (DEPTH, DEC_BATCH, WINDOW, N_KV_HEADS, HEAD_DIM), 1.0),
        "cache_v": nrm(ks[3], (DEPTH, DEC_BATCH, WINDOW, N_KV_HEADS, HEAD_DIM), 0.5),
        "state_conv": nrm(ks[4], (DEPTH, DEC_BATCH, CONV_WIDTH - 1, CONV_CH), 0.5),
        "w_in": nrm(ks[5], (DEPTH, D_MODEL, IN_DIM), D_MODEL ** -0.5) * col_scale,
        "b_in": nrm(ks[6], (DEPTH, IN_DIM), 0.02),
        "sinks": nrm(ks[7], (DEPTH, N_HEADS), 1.0),
        "conv_w": nrm(ks[8], (DEPTH, CONV_WIDTH, CONV_CH), CONV_WIDTH ** -0.5),
        "conv_b": nrm(ks[9], (DEPTH, CONV_CH), 0.02),
        "ln_conv_g": 1.0 + nrm(ks[10], (DEPTH, CONV_CH), 0.05),
        "ln_conv_b": nrm(ks[11], (DEPTH, CONV_CH), 0.02),
        "w_out": nrm(ks[12], (DEPTH, MIX_DIM, D_MODEL), MIX_DIM ** -0.5) * BETA,
        "b_out": nrm(ks[13], (DEPTH, D_MODEL), 0.02),
        "ln1_g": 1.0 + nrm(ks[14], (DEPTH, D_MODEL), 0.05),
        "ln1_b": nrm(ks[15], (DEPTH, D_MODEL), 0.02),
        "w_router_group": nrm(ks[16], (DEPTH, D_MODEL, N_GROUPS), D_MODEL ** -0.5),
        "w_router_expert": nrm(ks[17], (DEPTH, D_MODEL, N_GROUPS, EXPERTS_PER_GROUP), D_MODEL ** -0.5),
        "w1": nrm(ks[18], (DEPTH, N_EXPERTS, D_MODEL, D_FF_EXPERT), D_MODEL ** -0.5),
        "w3": nrm(ks[19], (DEPTH, N_EXPERTS, D_MODEL, D_FF_EXPERT), D_MODEL ** -0.5),
        "w2": nrm(ks[20], (DEPTH, N_EXPERTS, D_FF_EXPERT, D_MODEL), D_FF_EXPERT ** -0.5) * BETA,
        "ln2_g": 1.0 + nrm(ks[21], (DEPTH, D_MODEL), 0.05),
        "ln2_b": nrm(ks[22], (DEPTH, D_MODEL), 0.02),
    }

def reference(x_prompt, x_sample, cache_k, cache_v, state_conv, w_in, b_in, sinks, conv_w, conv_b,
              ln_conv_g, ln_conv_b, w_out, b_out, ln1_g, ln1_b, w_router_group, w_router_expert,
              w1, w3, w2, ln2_g, ln2_b):
    pos_p = jnp.arange(x_prompt.shape[1])
    pos_s = PAST_LEN + jnp.arange(x_sample.shape[1])
    zero_prefix = jnp.zeros((x_prompt.shape[0], CONV_WIDTH - 1, CONV_CH), x_prompt.dtype)
    yp, ys = x_prompt, x_sample
    kp_l, vp_l, cp_l, ks_l, vs_l, cs_l = [], [], [], [], [], []
    for l in range(DEPTH):
        params = (w_in[l], b_in[l], sinks[l], conv_w[l], conv_b[l], ln_conv_g[l], ln_conv_b[l],
                  w_out[l], b_out[l], ln1_g[l], ln1_b[l], w_router_group[l], w_router_expert[l],
                  w1[l], w3[l], w2[l], ln2_g[l], ln2_b[l])
        yp, kp, vp, cp = decoder_layer(yp, pos_p, None, None, zero_prefix, *params)
        ys, k_s, v_s, c_s = decoder_layer(ys, pos_s, cache_k[l], cache_v[l], state_conv[l], *params)
        kp_l.append(kp); vp_l.append(vp); cp_l.append(cp)
        ks_l.append(k_s); vs_l.append(v_s); cs_l.append(c_s)
    new_k_prompt = jnp.stack(kp_l)
    new_v_prompt = jnp.stack(vp_l)
    new_conv_prompt = jnp.stack(cp_l)
    new_k_sample = jnp.stack(ks_l)
    new_v_sample = jnp.stack(vs_l)
    new_conv_sample = jnp.stack(cs_l)
    return (yp, ys, new_k_prompt, new_v_prompt, new_conv_prompt, new_k_sample, new_v_sample, new_conv_sample)


_drawn_inputs = setup_inputs


def setup_inputs(seed=0):
    import zlib

    import numpy as np

    out = dict(_drawn_inputs(seed))
    spreads = {}
    factors = {'sinks': 59.807,
     'conv_b': 4.322,
     'ln_conv_g': 3.164,
     'ln_conv_b': 7.161,
     'ln2_b': 2.834,
     'b_out': 3.217}
    for name, (base, spread) in spreads.items():
        noise = np.random.default_rng([zlib.crc32(name.encode()), seed]).standard_normal(out[name].shape)
        drawn = base * np.exp(spread * noise) if base else spread * noise
        out[name] = __import__('jax').numpy.asarray(drawn.astype(out[name].dtype))
    for name, factor in factors.items():
        out[name] = (out[name] * factor).astype(out[name].dtype)
    return out
```

```python
from contextlib import ExitStack

import numpy as np

import concourse.bass as bass
from concourse import mybir

F32 = mybir.dt.float32
I32 = mybir.dt.int32
U32 = mybir.dt.uint32
ALU = mybir.AluOpType
ACT = mybir.ActivationFunctionType
AX = mybir.AxisListType.X

P = 128
D = 1024
SEQ = 2048
DEC = 8
HEADS, KVH, HD = 8, 2, 64
G = HEADS // KVH
HALF = HD // 2
AD = HEADS * HD
KVD = KVH * HD
WIN = 128
CH = D - AD
TAPS = 31
IN = AD + 2 * KVD + 2 * CH
NG, EPG = 4, 8
NE = NG * EPG
FF = 256
EPS = 1e-5
ALPHA = 2.0 ** 0.25
SCALE = HD ** -0.5
NEG = -1e30
PAST = 16384

PARTS = {"q": (0, AD), "kv": (AD, AD + 2 * KVD), "ca": (AD + 2 * KVD, AD + 2 * KVD + CH), "cg": (IN - CH, IN)}
KD = D // P
CC = CH // P
NT = SEQ // P
TOK = SEQ + DEC
PAIRS = 2 * TOK
NB = (PAIRS + NE * (P - 1)) // P
RING = 3
WCOLS = 2 * KD * FF + 2 * D
BATCH, BATCHES = 4, 3
TAIL = 25
FILLS = 3
SETS = 4
assert NT % SETS == 0
assert NB % RING == 0
MAXC = -(-TOK // P)
NBT = 64
assert NB <= NBT

_c = {}
_n = 0
for _name, _w in (("ident", P), ("before", P), ("ones", P), ("band", 2 * P), ("band0", 2 * P), ("iota", P),
                  ("rope", (NT + 1) * 2 * HALF), ("tok", NT + 1), ("thresh", MAXC), ("mhalf", 1), ("slot_step", NE)):
    _c[_name] = (_n, _n + _w)
    _n += _w
NCONST = _n


def constants():
    c = np.zeros((P, NCONST), np.float32)

    def put(name, value):
        a, b = _c[name]
        c[:, a:b] = value

    i = np.arange(P)
    put("ident", np.eye(P, dtype=np.float32))
    put("before", (i[:, None] < i[None, :]).astype(np.float32))
    put("ones", 1.0)
    prev = np.where(i[None, :] > i[:, None], 0.0, NEG)
    cur = np.where(i[None, :] <= i[:, None], 0.0, NEG)
    put("band", np.concatenate([prev, cur], 1))
    put("band0", np.concatenate([np.full((P, P), NEG), cur], 1))
    put("iota", i[None, :])
    inv = np.float32(10000.0) ** (-np.arange(HALF, dtype=np.float32) / np.float32(HALF))
    pos = np.concatenate([np.arange(SEQ), np.full(P, PAST)]).astype(np.float32)
    ang = (pos[:, None] * inv.astype(np.float32)).astype(np.float32)
    table = np.concatenate([np.cos(ang), np.sin(ang)], 1).astype(np.float32)
    put("rope", table.reshape(NT + 1, P, 2 * HALF).transpose(1, 0, 2).reshape(P, -1))
    put("tok", np.arange(NT + 1)[None, :] * P + i[:, None])
    put("thresh", P * np.arange(MAXC)[None, :])
    put("mhalf", -0.5)
    slot = np.arange(NE + 1) % RING * WCOLS
    put("slot_step", (slot[1:] - slot[:-1])[None, :])
    return c


def after(eng, sem, tile, last=None, per=1):
    if isinstance(tile, int):
        if last is not None:
            tile = min(tile, last)
        if tile < 0:
            return
    eng.wait_ge(sem, (tile + 1) * per)


SEMS = """
zlin_ok conv0_ok prod_ok prod_used li_ok fill_out out1_ev const_in w_q_in w_kv_in w_ca_in w_cg_in w_out_in
x_in xres_in convw_in pe_xT pe_inq pe_inkv pe_inca pe_incg pe_qT pe_kT pe_uT pe_scA pe_scB pe_ptA pe_ptB
pe_pvA pe_pvB pe_yN pe_zT pe_atT pe_out0 pe_out1 pe_hT pe_router pe_rank pe_cwT xT_ev qT_ev kT_ev uT_ev hT_ev
atT_ev ptA_ev ptB_ev z_ev inq_ev inkv_ev inca_ev incg_ev rope_q rope_k glu_sig u_ok v_ok scA_ev nmA_ok expA_ok
scB_ev nmB_ok expB_ok pv_ev es_ok l_ok tail_ok conv_ok cstat_ok cnm_ok zsig_ok mixc_ok xres_ok out0_ev r_ok
lstat_ok lnm_ok lz_ok lg_ok h_ok h_out ro_ev ro_nm ro_e1 ro_d ro_e2 onehot_ok rk_ev cw_ok init_ok g_init k_out
v_out u_out s_state s_ks s_vs s_sinks s_u29 s_k127 s_v127 s_kc pe_sA sA_ev pe_sB sB_ev pe_sC pe_sD sD_ev sm_ok
s_exp s_p pe_sF s_fin tab_build pe_tab tab_ok eids_ok idx_ok xg_in0 xg_in1 xg_in2 w0_ld w1_ld w2_ld y_out0
y_out1 y_out2 pe_xg pe_up pe_gT pe_dn xgT_ev a_sig g_ok gT_ev y_ev0 y_ev1 ln2_in i_c c_g0 c_g1 c_g2 c_g3 c_h0
c_h1 c_h2 c_h3 c_o0 c_o1 c_o2 c_o3 c_st c_nm c_z c_m c_y
""".split()


def layer(nc, a, o, scratch):
    with ExitStack() as ctx:
        s = {n: ctx.enter_context(nc.semaphore(n)) for n in SEMS}

        def sb(name, cols, dt=F32, rows=P):
            return ctx.enter_context(nc.sbuf_tensor(name, [rows, cols], dt))

        def view(buf, **dims):
            names = list(dims)
            return buf.rearrange(f"p ({' '.join(names)}) -> p {' '.join(names)}", **dims)

        wmem = sb("wmem", KD * (IN + D))
        w_in_mem, w_out_mem = wmem[:, 0:KD * IN], wmem[:, KD * IN:]
        assert 2 * WCOLS <= KD * IN and RING * WCOLS <= KD * (IN + D)
        fills = FILLS * (NT - 5)
        assert NB - fills <= PAIRS // P + 1
        const = sb("const", NCONST)
        C = {n: const[:, x:y] for n, (x, y) in _c.items()}
        ln_g = sb("ln_g", D)
        ln_b = sb("ln_b", D)
        b_in = sb("b_in", IN)
        b_out = sb("b_out", D)
        wr = sb("wr", KD * (NG + NE))
        wr_v = view(wr[:, :], k=KD, n=NG + NE)
        nsink = sb("nsink", HEADS)
        expert = sb("expert", 2 * (NT + 1))
        gate = sb("gate", 2 * (NT + 1))
        rank = sb("rank", 2 * (NT + 1))
        slot_i = sb("slot_i", 2 * (NT + 1), I32)
        counts = sb("counts", NE)

        work_cols = 20000
        work = sb("work", work_cols)
        used = [0]

        def take(cols):
            at = used[0]
            used[0] += cols
            assert used[0] <= work_cols, used[0]
            return work[:, at:at + cols]

        w_in = view(w_in_mem, k=KD, n=IN)
        w_out = view(w_out_mem, k=KD, n=D)

        x = take(D)
        xT = view(take(D), k=KD, t=P)
        qk = take(AD + KVD)
        rot_c = take(AD + KVD)
        rot_s = take(AD + KVD)
        q_r = take(AD)
        k_r = take(KVD)
        v_next = take(KVD)
        V2 = view(take(2 * KVD), w=2, n=KVD)
        qT = view(take(AD), g=G, t=P)
        kT2 = take(2 * P)
        ca = take(CH)
        cg = take(CH)
        u = take(CH)
        uT = view(take(CC * (TAPS - 1 + P)), c=CC, t=TAPS - 1 + P)
        conv = view(take(CC * P), c=CC, t=P)
        z = take(CH)
        zsig = view(take(CC * P), c=CC, t=P)
        zlin = view(take(CC * P), c=CC, t=P)
        smA = view(take(G * 2 * P), h=G, s=2 * P)
        smB = view(take(G * 2 * P), h=G, s=2 * P)
        ptA = view(take(G * 2 * P), h=G, w=2, t=P)
        ptB = view(take(G * 2 * P), h=G, w=2, t=P)
        attn = take(AD)
        mixT = view(take(KD * P), k=KD, t=P)
        xres = take(D)
        r = take(D)
        hT = view(take(D), k=KD, t=P)
        cw = view(take(CC * (TAPS + 3)), c=CC, j=TAPS + 3)
        sm = take(160)
        mx, nm, rs, es, dd, li = (sm[:, 8 * i:8 * i + 8] for i in range(6))
        cst6, cmv, crs, cnm, cve = sm[:, 48:54], sm[:, 54:56], sm[:, 56:57], sm[:, 57:58], sm[:, 58:59]
        lst, lmv, lrs, lnm, lve = sm[:, 60:72], sm[:, 72:74], sm[:, 74:75], sm[:, 75:76], sm[:, 76:77]
        lg8, g8, v8 = sm[:, 80:88], sm[:, 88:96], sm[:, 96:104]
        gidx, ngm, gsum, rd, re2, rr, pen = (sm[:, 104:105], sm[:, 105:106], sm[:, 106:107], sm[:, 107:108],
                                             sm[:, 108:109], sm[:, 109:110], sm[:, 112:116])
        eg4 = sm[:, 116:120]
        e2s, g2s, r2s = sm[:, 120:122], sm[:, 122:124], sm[:, 124:126]
        carry = sm[:, 126:127]
        le = take(NE)
        oh1, oh2, ohs, rk = take(NE), take(NE), take(NE), take(NE)
        ttr_out = take(NE)
        tail = view(take(CC * (TAPS - 1)), c=CC, t=TAPS - 1)
        gi_u = sb("gi_u", 8, U32)
        prods = view(sb("prods", BATCH * CC * P)[:, :], b=BATCH, c=CC, t=P)
        ei_u = sb("ei_u", 8, U32)

        bank_T = ctx.enter_context(nc.psum_tensor("bank_T", [P, 1024], F32))
        bank_S = ctx.enter_context(nc.psum_tensor("bank_S", [P, 1024], F32))
        P0 = ctx.enter_context(nc.psum_tensor("P0", [P, 512], F32))
        P1 = ctx.enter_context(nc.psum_tensor("P1", [P, 512], F32))
        M0 = ctx.enter_context(nc.psum_tensor("M0", [P, 512], F32))
        M1 = ctx.enter_context(nc.psum_tensor("M1", [P, 512], F32))
        T8 = view(bank_T[:, :], k=KD, t=P)

        UP = [P0, P1, M1]
        used[0] = 0
        xg = [take(D) for _ in range(RING)]
        xgT = view(take(D), k=KD, t=P)
        sg = take(FF)
        gs = take(FF)
        gu = take(FF)
        gT = view(take(FF), k=2, t=P)
        ye = take(RING * D)
        ge = [take(D), take(D)]
        table_g = take(NBT)
        cum, startb, nblk = take(NE), take(NE), take(NE)
        cmpb = take(NE * MAXC)
        bexp = take(NBT * NE)
        bex = take(NBT)
        used_b, woff = take(NBT), take(NBT)
        bstep = take(NBT * NE)
        oh34 = take(2 * (NT + 1) * NE)
        st34, lof, hif, slf = (take(2 * (NT + 1)) for _ in range(4))
        table_i = sb("table_i", NBT, I32)
        nblk_i = sb("nblk_i", 1, I32)
        bex_i = sb("bex_i", NBT, I32)
        woff_i = sb("woff_i", NBT, I32)
        cum_i = sb("cum_i", NE, I32)
        lo_i = sb("lo_i", 2 * (NT + 1), I32)
        hi_i = sb("hi_i", 2 * (NT + 1), I32)
        gidx3 = sb("gidx3", RING, I32)
        cidx = sb("cidx", 2 * SETS, I32)
        tick = sb("tick", 64, rows=1)
        stores_f = sb("stores_f", RING)
        stores_i = sb("stores_i", RING, I32)
        c_small = sb("c_small", SETS * 20)
        c_st, c_mv, c_ve, c_rstd, c_nmr = ([c_small[:, q * 20 + x:q * 20 + y] for q in range(SETS)] for x, y in
                                           ((0, 12), (12, 14), (14, 15), (15, 16), (16, 17)))
        third = view(wmem[:, 0:SETS * 3 * D], q=SETS, w=3, n=D)
        cy = [[third[:, q, 0], third[:, q, 1]] for q in range(SETS)]
        chh = [third[:, q, 2] for q in range(SETS)]

        h_dram, y_dram = scratch
        ident = C["ident"]

        block = ctx.enter_context(nc.Block())

        ITER = (list(range(-1, 3)), (3, NT - 2), list(range(NT - 2, NT + 3)))

        def rows_of(tile):
            return DEC if isinstance(tile, int) and tile == NT else P

        def has(tile, last=NT):
            return not isinstance(tile, int) or 0 <= tile <= last

        def pipeline(eng, body, sample):
            for t in ITER[0]:
                body(t)
            with eng.Fori(*ITER[1]) as t:
                body(t)
            for t in ITER[2]:
                if t == NT:
                    sample()
                body(t)

        cwn = r[0:TAPS + 3, 0:CH]
        Ks = view(smA.rearrange("p h s -> p (h s)"), b=DEC, n=KVD)
        Vs = view(smB.rearrange("p h s -> p (h s)"), b=DEC, n=KVD)
        KsT = view(ptA.rearrange("p h w t -> p (h w t)"), b=DEC, s=WIN)
        state_n = view(ptB.rearrange("p h w t -> p (h w t)"), i=2, n=CH)
        ext = view(prods.rearrange("p b c t -> p (b c t)")[:, 0:CC * DEC * TAPS], c=CC, b=DEC, j=TAPS)
        prod = view(x[:, 0:CC * DEC * TAPS], c=CC, b=DEC, j=TAPS)
        smp = sb("smp", 480)
        zeros = smp[:, 0:256]
        qTs = view(smp[:, 0:32], g=G, b=DEC)
        sT = smp[:, 32:96]
        PTs = smp[:, 96:160]
        Ps = smp[0:64, 160:288]
        mix_s = view(smp[:, 288:320], g=G, b=DEC)
        conv_s = view(smp[:, 320:352], c=CC, b=DEC)
        s_mx, s_nm, s_rs, s_es, s_dd, s_li, s_ns = (smp[0:64, 352 + i:353 + i] for i in range(7))
        NROW = DEC * (TAPS - 1) // 2

        @block.sync
        def _(sp):
            sp.dma_start(x, a["x_prompt"][0:P, :]).then_inc(s["x_in"], 16)
            sp.dma_start(const[:, :], a["consts"]).then_inc(s["const_in"], 16)
            for part, (c0, c1) in PARTS.items():
                sp.dma_start(w_in[:, :, c0:c1], a["w_in"].rearrange("(p k) n -> p k n", k=KD)[:, :, c0:c1]
                             ).then_inc(s[f"w_{part}_in"], 16)
            for kv in range(KVH):
                src = a["w_out"][0:AD, :].rearrange("(kv g d) n -> kv d g n", kv=KVH, g=G)[kv]
                sp.dma_start(w_out[kv * HD:(kv + 1) * HD, 0:G, :], src).then_inc(s["w_out_in"], 16)
            sp.dma_start(w_out[:, G:KD, :],
                         a["w_out"][AD:D, :].rearrange("(c p) n -> p c n", p=P)).then_inc(s["w_out_in"], 16)

            def fill(b, sem):
                sp.dma_start(y_dram[bass.ds(b * P, P), :].rearrange("p (q n) -> p q n", n=256),
                             zeros.unsqueeze(1).broadcast_to([P, D // 256, 256])).then_inc(sem, 16)

            def load(e, q):
                at = q * WCOLS
                for m, name in enumerate(("w1", "w3", "w2")):
                    k = 2 if name == "w2" else KD
                    cols = D if name == "w2" else FF
                    if not isinstance(e, int):
                        sp.wait_ge(s["eids_ok"], 1)
                    if not isinstance(e, int) or e:
                        sp.wait_ge(s[f"w{m}_ld"], e * 16)
                    src = a[name][bass.ds(e, 1)].rearrange("e (p k) n -> (e p) (k n)", k=k)
                    sp.dma_start(wmem[:, at:at + k * cols], src).then_inc(s[f"w{m}_ld"], 16)
                    at += k * cols

            def step(t):
                if isinstance(t, int) and t == NT - 1:
                    after(sp, s["rope_k"], NT - 1)
                    sp.dma_start(o["new_k_prompt"], k_r).then_inc(s["k_out"], 16)
                    after(sp, s["inkv_ev"], NT - 1)
                    sp.dma_start(o["new_v_prompt"], v_next).then_inc(s["v_out"], 16)
                    after(sp, s["u_ok"], NT - 1)
                    sp.dma_start(o["new_conv_prompt"], u[P - TAPS + 1:P, :]).then_inc(s["u_out"], 16)
                if has(t + 2) and not (isinstance(t, int) and t + 2 < 1):
                    n = rows_of(t + 2)
                    after(sp, s["pe_xT"], t + 1)
                    src = a["x_sample"] if n == DEC else a["x_prompt"][bass.ds((t + 2) * P, P), :]
                    sp.dma_start(x[0:n, :], src).then_inc(s["x_in"], 16)
                if has(t - 1):
                    n = rows_of(t - 1)
                    after(sp, s["r_ok"], t - 2)
                    src = a["x_sample"] if n == DEC else a["x_prompt"][bass.ds((t - 1) * P, P), :]
                    sp.dma_start(xres[0:n, :], src).then_inc(s["xres_in"], 16)
                if not isinstance(t, int):
                    for b in range(FILLS):
                        fill(NB + (t - (NT - 2)) * FILLS + b, s["fill_out"])
                elif t == 2:
                    sp.wait_ge(s["g_init"], 1)
                    fill(NB - 1, s["y_out2"])
                if isinstance(t, int) and t == NT:
                    after(sp, s["pe_incg"], NT)
                    for e in range(2):
                        load(e, e)
                if has(t - 2):
                    n = rows_of(t - 2)
                    after(sp, s["h_ok"], t - 2)
                    dst = h_dram[SEQ:TOK, :] if n == DEC else h_dram[bass.ds((t - 2) * P, P), :]
                    sp.dma_start(dst, r[0:n, :]).then_inc(s["h_out"], 16)

            def sample():
                old = [("cache_k", "new_k_sample"), ("cache_v", "new_v_sample")]
                for src, dst in old:
                    sp.dma_start(o[dst][:, 0:WIN - 1, :], a[src][:, 1:WIN, :]).then_inc(s["s_kc"], 16)
                sp.dma_start(o["new_conv_sample"][:, 0:TAPS - 2, :],
                             a["state_conv"][:, 1:TAPS - 1, :]).then_inc(s["s_kc"], 16)
                after(sp, s["rope_k"], NT)
                sp.dma_start(o["new_k_sample"][:, WIN - 1, :], k_r[0:DEC, :]).then_inc(s["s_k127"], 16)
                after(sp, s["inkv_ev"], NT)
                sp.dma_start(o["new_v_sample"][:, WIN - 1, :], v_next[0:DEC, :]).then_inc(s["s_v127"], 16)
                after(sp, s["u_ok"], NT)
                sp.dma_start(o["new_conv_sample"][:, TAPS - 2, :], u[0:DEC, :]).then_inc(s["s_u29"], 16)
                after(sp, s["pe_ptB"], NT - 1)
                sp.dma_start(Ks[0:WIN - 1], a["cache_k"][:, 1:WIN, :].rearrange("b s n -> s b n")).then_inc(s["s_ks"], 16)
                sp.dma_start(Vs[0:WIN - 1], a["cache_v"][:, 1:WIN, :].rearrange("b s n -> s b n")).then_inc(s["s_vs"], 16)
                after(sp, s["pe_pvB"], NT - 1)
                for i in range(2):
                    src = a["state_conv"].rearrange("(i b) j n -> i (b j) n", i=2)[i]
                    sp.dma_start(state_n[0:NROW, i], src).then_inc(s["s_state"], 16)
                sp.wait_ge(s["s_k127"], 16)
                sp.dma_start(Ks[WIN - 1:WIN], o["new_k_sample"][:, WIN - 1:WIN, :].rearrange("b s n -> s b n")).then_inc(s["s_ks"], 16)
                sp.wait_ge(s["s_v127"], 16)
                sp.dma_start(Vs[WIN - 1:WIN], o["new_v_sample"][:, WIN - 1:WIN, :].rearrange("b s n -> s b n")).then_inc(s["s_vs"], 16)

            pipeline(sp, step, sample)

            after(sp, s["h_ok"], NT)
            sp.dma_start(ln_g[:, :], a["ln2_g"].partition_broadcast(P)).then_inc(s["ln2_in"], 16)
            sp.dma_start(ln_b[:, :], a["ln2_b"].partition_broadcast(P)).then_inc(s["ln2_in"], 16)

            after(sp, s["pe_out1"], NT)
            load(2, 2)
            sp.wait_ge(s["eids_ok"], 1)
            n_blocks = sp.value_load(nblk_i[0:1, :], min_val=PAIRS // P + 1, max_val=NB)

            def replace(e, q):
                done = sp.value_load(cum_i[0:1, bass.ds(e - RING, 1)], min_val=1, max_val=NB + 1)
                sp.wait_ge(s["eids_ok"], 1)
                sp.wait_ge(s["pe_dn"], done)
                load(e, q)

            with sp.Fori(1, NE // RING) as i:
                for q in range(RING):
                    replace(i * RING + q, q)
            for e in range(NE // RING * RING, NE):
                replace(e, e % RING)

            def fetch(t, q, n):
                src = h_dram[SEQ:TOK, :] if n == DEC else h_dram[bass.ds(t * P, P), :]
                sp.dma_start(chh[q][0:n, :], src).then_inc(s[f"c_h{q}"], 16)

            def store(t, q, n):
                sp.wait_ge(s["c_y"], t + 1)
                dst = o["y_sample"] if n == DEC else o["y_prompt"][bass.ds(t * P, P), :]
                sp.dma_start(dst, cy[q][1][0:n, :]).then_inc(s[f"c_o{q}"], 16)

            for m in range(3):
                sp.wait_ge(s[f"w{m}_ld"], 16 * NE)
            after(sp, s["pe_dn"], n_blocks)
            for t in range(SETS):
                fetch(t, t, P)
            with sp.Fori(0, NT // SETS - 1) as i:
                for q in range(SETS):
                    store(i * SETS + q, q, P)
                    fetch(i * SETS + q + SETS, q, P)
            for t in range(NT - SETS, NT + 1):
                store(t, t % SETS, rows_of(t))
                if t + SETS == NT:
                    fetch(NT, 0, DEC)
            for sem, v in (("k_out", 1), ("v_out", 1), ("u_out", 1), ("s_kc", 3), ("s_k127", 1), ("s_v127", 1),
                           ("s_u29", 1), ("c_o0", NT // SETS + 1), ("c_o1", NT // SETS), ("c_o2", NT // SETS),
                           ("c_o3", NT // SETS), ("h_out", NT + 1)):
                sp.wait_ge(s[sem], 16 * v)

        @block.tensor
        def _(pe):
            mm, tr = nc.tensor.matmul, nc.tensor.transpose

            def pass_a(dst, part, rows, tile):
                c0, c1 = PARTS[part]
                n = c1 - c0
                if isinstance(tile, int) and tile == 0:
                    pe.wait_ge(s[f"w_{part}_in"], 16)
                for k in range(KD):
                    last = mm(dst[0:rows, 0:n], xT[:, k, 0:rows], w_in[:, k, c0:c0 + n],
                              start=(k == 0), stop=(k == KD - 1))
                return last

            def scores(kv, sem):
                for g in range(G):
                    last = mm(bank_S[:, g * 2 * P:(g + 1) * 2 * P], qT[kv * HD:(kv + 1) * HD, g, :],
                              kT2[kv * HD:(kv + 1) * HD, :], start=True, stop=True)
                last.then_inc(sem, 1)

            def flip(sm_h, sem):
                for g in range(G):
                    for w in range(2):
                        last = tr(T8[:, 2 * g + w, :], sm_h[:, g, w * P:(w + 1) * P], ident)
                last.then_inc(sem, 1)

            def values(kv, pt, sem):
                for g in range(G):
                    for w in range(2):
                        last = mm(M0[:, (kv * G + g) * HD:(kv * G + g + 1) * HD], pt[:, g, w, :],
                                  V2[:, w, kv * HD:(kv + 1) * HD], start=(w == 0), stop=(w == 1))
                last.then_inc(sem, 1)

            def project(half, dst, rows, tile):
                for k in range(KD):
                    if k == G and half == 0:
                        after(pe, s["mixc_ok"], tile)
                    mix = mix_s[:, k, :] if k < G and rows == DEC else mixT[:, k, 0:rows]
                    last = mm(dst[0:rows, :], mix, w_out[:, k, half * 512:(half + 1) * 512],
                              start=(k == 0), stop=(k == KD - 1))
                return last

            pe.wait_ge(s["const_in"], 16)
            pe.wait_ge(s["convw_in"], 80)
            for c in range(CC):
                last = tr(M1[:, c * (TAPS + 3):(c + 1) * (TAPS + 3)], cwn[:, c * P:(c + 1) * P],
                          ident[0:TAPS + 3, 0:TAPS + 3])
            last.then_inc(s["pe_cwT"], 1)

            def step(t):
                A, B, Cc, Dd = has(t + 1), has(t, NT - 1), has(t - 1), has(t - 2)
                na, nc_, nd = rows_of(t + 1), rows_of(t - 1), rows_of(t - 2)
                if A:
                    pe.wait_ge(s["x_in"], (t + 2) * 16)
                    after(pe, s["ptB_ev"], t - 1)
                    for k in range(KD):
                        last = tr(T8[:, k, 0:na], x[0:na, k::KD], ident[0:na, 0:na])
                    last.then_inc(s["pe_xT"], 1)
                if B:
                    after(pe, s["rope_q"], t)
                    after(pe, s["rope_k"], t)
                    after(pe, s["pv_ev"], t - 1)
                    after(pe, s["scB_ev"], t - 1)
                    for g in range(G):
                        last = tr(M0[:, g * P:(g + 1) * P], q_r[:, g * P:(g + 1) * P], ident)
                    last.then_inc(s["pe_qT"], 1)
                    tr(bank_S[:, 0:P], k_r, ident).then_inc(s["pe_kT"], 1)
                    after(pe, s["u_ok"], t)
                    for c in range(CC):
                        last = tr(bank_S[:, 512 + c * P:512 + (c + 1) * P], u[:, c * P:(c + 1) * P], ident)
                    last.then_inc(s["pe_uT"], 1)
                if A:
                    after(pe, s["xT_ev"], t + 1)
                    after(pe, s["inca_ev"], t)
                    after(pe, s["out0_ev"], t - 2)
                    pass_a(P0, "q", na, t + 1).then_inc(s["pe_inq"], 1)
                if B:
                    after(pe, s["qT_ev"], t)
                    after(pe, s["kT_ev"], t)
                    after(pe, s["uT_ev"], t)
                    scores(0, s["pe_scA"])
                if Cc:
                    after(pe, s["atT_ev"], t - 1, NT - 1)
                    after(pe, s["zlin_ok"], t - 2)
                    after(pe, s["conv_ok"], t - 1)
                    if isinstance(t, int) and t - 1 == 0:
                        pe.wait_ge(s["cw_ok"], 1)
                    for c in range(CC):
                        src = conv_s[:, c, :] if nc_ == DEC else conv[:, c, :]
                        last = tr(M1[0:nc_, c * P:(c + 1) * P], src, ident)
                    last.then_inc(s["pe_yN"], 1)
                if Dd:
                    after(pe, s["xT_ev"], t + 1, NT)
                    after(pe, s["h_ok"], t - 2)
                    if not A:
                        after(pe, s["hT_ev"], t - 3)
                    for k in range(KD):
                        last = tr(T8[:, k, 0:nd], r[0:nd, k::KD], ident[0:nd, 0:nd])
                    last.then_inc(s["pe_hT"], 1)
                if A:
                    after(pe, s["incg_ev"], t)
                    after(pe, s["out1_ev"], t - 2)
                    pass_a(P1, "kv", na, t + 1).then_inc(s["pe_inkv"], 1)
                if Cc:
                    after(pe, s["z_ev"], t - 1)
                    for c in range(CC):
                        last = tr(M1[:, c * P:c * P + nc_], z[0:nc_, c * P:(c + 1) * P], ident[0:nc_, 0:nc_])
                    last.then_inc(s["pe_zT"], 1)
                if Dd:
                    after(pe, s["hT_ev"], t - 2)
                    after(pe, s["qT_ev"], t, NT - 1)
                    if not B:
                        after(pe, s["rk_ev"], t - 3)
                        pe.wait_ge(s["s_fin"], 1)
                    for k in range(KD):
                        last = mm(M0[0:nd, 0:NG + NE], hT[:, k, 0:nd], wr_v[:, k, :],
                                  start=(k == 0), stop=(k == KD - 1))
                    last.then_inc(s["pe_router"], 1)
                if B:
                    after(pe, s["expA_ok"], t)
                    after(pe, s["hT_ev"], t - 2)
                    after(pe, s["xT_ev"], t + 1)
                    flip(smA, s["pe_ptA"])
                    after(pe, s["scA_ev"], t)
                    scores(1, s["pe_scB"])
                if A:
                    after(pe, s["inq_ev"], t + 1)
                    pass_a(P0, "ca", na, t + 1).then_inc(s["pe_inca"], 1)
                    after(pe, s["inkv_ev"], t + 1)
                    pass_a(P1, "cg", na, t + 1).then_inc(s["pe_incg"], 1)
                if Dd:
                    after(pe, s["onehot_ok"], t - 2)
                    after(pe, s["ro_ev"], t - 2)
                    mm(M0[0:nd, 0:NE], C["before"][0:nd, 0:nd], ohs[0:nd, :], start=True, stop=True)
                    mm(M0[:, NE:2 * NE], C["ones"][0:nd, :], ohs[0:nd, :], start=True,
                       stop=True).then_inc(s["pe_rank"], 1)
                if B:
                    after(pe, s["expB_ok"], t)
                    after(pe, s["ptA_ev"], t)
                    flip(smB, s["pe_ptB"])
                if Cc:
                    if isinstance(t, int) and t == 1:
                        pe.wait_ge(s["w_out_in"], 48)
                    after(pe, s["inca_ev"], t + 1, NT)
                    after(pe, s["out0_ev"], t - 2)
                    after(pe, s["atT_ev"], t - 1, NT - 1)
                    project(0, P0, nc_, t - 1).then_inc(s["pe_out0"], 1)
                if B:
                    after(pe, s["v_ok"], t)
                    after(pe, s["rk_ev"], t - 2)
                    values(0, ptA, s["pe_pvA"])
                    after(pe, s["ptB_ev"], t)
                    values(1, ptB, s["pe_pvB"])
                if Cc:
                    after(pe, s["incg_ev"], t + 1, NT)
                    after(pe, s["out1_ev"], t - 2)
                    project(1, P1, nc_, t - 1).then_inc(s["pe_out1"], 1)
                if B:
                    after(pe, s["pv_ev"], t)
                    after(pe, s["zlin_ok"], t - 1)
                    if isinstance(t, int) and t == 0:
                        pe.wait_ge(s["cw_ok"], 1)
                    for g in range(G):
                        last = tr(M1[:, g * P:(g + 1) * P], attn[:, g * P:(g + 1) * P], ident)
                    last.then_inc(s["pe_atT"], 1)

            def sample():
                after(pe, s["ptB_ev"], NT - 1)
                after(pe, s["scB_ev"], NT - 1)
                after(pe, s["pv_ev"], NT - 1)
                after(pe, s["atT_ev"], NT - 1)
                after(pe, s["rope_q"], NT)
                after(pe, s["u_ok"], NT)
                pe.wait_ge(s["s_ks"], 32)
                for b in range(DEC):
                    tr(T8[:, b, :], Ks[:, b, :], ident)
                for g in range(G):
                    tr(M0[:, g * DEC:(g + 1) * DEC], q_r[0:DEC, g * P:(g + 1) * P], ident[0:DEC, 0:DEC])
                for c in range(CC):
                    tr(M0[:, 64 + c * DEC:64 + (c + 1) * DEC], u[0:DEC, c * P:(c + 1) * P], ident[0:DEC, 0:DEC])
                pe.wait_ge(s["s_state"], 32)
                for c in range(CC):
                    for i in range(2):
                        at = (c // 2) * 512 + (c % 2) * 2 * NROW + i * NROW
                        last = tr(bank_S[:, at:at + NROW], state_n[0:NROW, i, c * P:(c + 1) * P],
                                  ident[0:NROW, 0:NROW])
                last.then_inc(s["pe_sA"], 1)
                pe.wait_ge(s["sA_ev"], 1)
                for b in range(DEC):
                    for kv in range(KVH):
                        half = slice(kv * HD, (kv + 1) * HD)
                        dst = (M1, bank_S)[kv][:, b * G:(b + 1) * G]
                        last = mm(dst, KsT[half, b, :], qTs[half, :, b], start=True, stop=True)
                last.then_inc(s["pe_sB"], 1)
                pe.wait_ge(s["sB_ev"], 1)
                tr(M0[0:64, 128:256], sT, ident).then_inc(s["pe_sC"], 1)
                pe.wait_ge(s["s_p"], 1)
                tr(M1[:, 128:192], Ps, ident[0:64, 0:64]).then_inc(s["pe_sD"], 1)
                pe.wait_ge(s["sD_ev"], 1)
                pe.wait_ge(s["s_vs"], 32)
                for b in range(DEC):
                    last = mm(M0[:, 256 + b * HEADS:256 + (b + 1) * HEADS], Vs[:, b, :],
                              PTs[:, b * HEADS:(b + 1) * HEADS], start=True, stop=True)
                last.then_inc(s["pe_sF"], 1)
                pe.wait_ge(s["s_fin"], 1)

            pipeline(pe, step, sample)

            after(pe, s["rk_ev"], NT)
            for t in range(NT + 1):
                n = rows_of(t)
                pe.wait_ge(s["tab_build"], t + 1)
                for k in range(2):
                    b0 = ge[t % 2][0:n, k * 256:(k + 1) * 256]
                    last = mm(M0[:, 0:2 * NBT], b0[:, 0:P], b0[:, P:2 * P], start=(t == 0 and k == 0),
                              stop=(t == NT and k == 1))
                    if t == 0 and k == 0:
                        last.then_inc(s["pe_dn"], 1)
                last.then_inc(s["pe_tab"], 1)

            n_blocks = pe.value_load(nblk_i[0:1, :], min_val=PAIRS // P + 1, max_val=NB)

            def turn(b, j, i):
                pe.wait_ge(s[f"xg_in{j}"], 16 * (i + 1))
                after(pe, s["xgT_ev"], b - 1)
                for k in range(KD):
                    last = tr(T8[:, k, :], xg[j][:, k::KD], ident)
                last.then_inc(s["pe_xg"], 1)

            def up(b, j, i):
                loaded = pe.value_load(bex_i[0:1, bass.ds(b, 1)], min_val=16, max_val=16 * NE)
                off = pe.value_load(woff_i[0:1, bass.ds(b, 1)], min_val=0, max_val=(RING - 1) * WCOLS)
                after(pe, s["xgT_ev"], b)
                for m in range(3):
                    pe.wait_ge(s[f"w{m}_ld"], loaded)
                after(pe, s["g_ok"], b - RING)
                both = wmem[:, bass.ds(off, 2 * KD * FF)].rearrange("p (m k f) -> p k m f", m=2, k=KD)
                for k in range(KD):
                    last = mm(UP[j][:, :].rearrange("p (m f) -> p m f", m=2), xgT[:, k, :], both[:, k],
                              start=(k == 0), stop=(k == KD - 1))
                last.then_inc(s["pe_up"], 1)

            def turn_g(b):
                after(pe, s["g_ok"], b)
                after(pe, s["gT_ev"], b - 1)
                for k in range(2):
                    last = tr(M0[:, k * P:(k + 1) * P], gu[:, k::2], ident)
                last.then_inc(s["pe_gT"], 1)

            def down(b):
                off = pe.value_load(woff_i[0:1, bass.ds(b, 1)], min_val=0, max_val=(RING - 1) * WCOLS)
                after(pe, s["gT_ev"], b)
                after(pe, s["y_ev0"], b - 1)
                after(pe, s["y_ev1"], b - 1)
                for half in range(2):
                    for k in range(2):
                        last = mm(bank_S[:, half * 512:(half + 1) * 512], gT[:, k, :],
                                  wmem[:, bass.ds(off + 2 * KD * FF + k * D + half * 512, 512)],
                                  start=(k == 0), stop=(k == 1))
                last.then_inc(s["pe_dn"], 1)

            pe.wait_ge(s["tab_ok"], 1)
            turn(0, 0, 0)
            pe.wait_ge(s["eids_ok"], 1)
            for b in range(RING):
                up(b, b, 0)
                if b:
                    turn_g(b - 1)
                turn(b + 1, (b + 1) % RING, (b + 1) // RING)
                if b:
                    down(b - 1)
            with pe.Fori(1, NB // RING) as i:
                for j in range(RING):
                    b = i * RING + j
                    with pe.If(b < n_blocks):
                        up(b, j, i)
                    with pe.If(b - 1 < n_blocks):
                        turn_g(b - 1)
                    with pe.If(b + 1 < n_blocks):
                        turn(b + 1, (j + 1) % RING, i + (j + 1) // RING)
                    with pe.If(b - 1 < n_blocks):
                        down(b - 1)
            with pe.If(NB - 1 < n_blocks):
                turn_g(NB - 1)
                down(NB - 1)

        @block.scalar
        def _(act):
            fn = nc.scalar.activation
            act.dma_start(cwn[0:TAPS, :], a["conv_w"]).then_inc(s["convw_in"], 16)
            for i, n in enumerate(("conv_b", "ln_conv_g", "ln_conv_b")):
                act.dma_start(cwn[TAPS + i:TAPS + i + 1, :], a[n]).then_inc(s["convw_in"], 16)
            act.dma_start(b_in[:, :], a["b_in"].partition_broadcast(P)).then_inc(s["convw_in"], 16)
            act.dma_start(nsink[:, :], a["sinks"].partition_broadcast(P)).then_inc(s["s_sinks"], 16)
            for b in range(DEC):
                act.dma_start(s_ns[b * HEADS:(b + 1) * HEADS, :], a["sinks"].rearrange("a h -> h a")).then_inc(s["s_sinks"], 16)
            act.dma_start(wr_v[:, :, 0:NG], a["w_router_group"].rearrange("(p k) n -> p k n", k=KD)).then_inc(s["init_ok"], 16)
            act.dma_start(wr_v[:, :, NG:], a["w_router_expert"].rearrange("(p k) n -> p k n", k=KD)).then_inc(s["init_ok"], 16)
            act.dma_start(b_out[:, :], a["b_out"].partition_broadcast(P)).then_inc(s["init_ok"], 16)
            act.dma_start(ln_g[:, :], a["ln1_g"].partition_broadcast(P)).then_inc(s["init_ok"], 16)
            act.dma_start(ln_b[:, :], a["ln1_b"].partition_broadcast(P)).then_inc(s["init_ok"], 16)

            def products(t, n):
                after(act, s["prod_used"], t * BATCHES + n - 1)
                for b in range(BATCH):
                    j = 1 + BATCH * n + b
                    for c in range(CC):
                        last = fn(prods[:, b, c, :], uT[:, c, j:j + P], ACT.Copy, scale=cw[:, c, j:j + 1])
                last.then_inc(s["prod_ok"], 1)

            def exps(smx, c0, sem_in, sem_out, t):
                after(act, sem_in, t)
                for g in range(G):
                    last = fn(smx[:, g, :], smx[:, g, :], ACT.Exp, bias=nm[:, c0 + g:c0 + g + 1], scale=SCALE,
                              accum_out=rs[:, c0 + g:c0 + g + 1])
                last.then_inc(sem_out, 1)

            def step(t):
                A, B, Cc, Dd = has(t + 1), has(t, NT - 1), has(t - 1), has(t - 2)
                na, nc_, nd = rows_of(t + 1), rows_of(t - 1), rows_of(t - 2)
                if A:
                    after(act, s["pe_xT"], t + 1)
                    after(act, s["pe_incg"], t)
                    fn(xT[:, :, 0:na], T8[:, :, 0:na], ACT.Copy).then_inc(s["xT_ev"], 1)
                if B:
                    after(act, s["pe_qT"], t)
                    after(act, s["pe_scB"], t - 1)
                    fn(qT.rearrange("p g t -> p (g t)"), M0[:, :], ACT.Copy).then_inc(s["qT_ev"], 1)
                    if isinstance(t, int) and t == 0:
                        act.wait_ge(s["g_init"], 1)
                    fn(kT2[:, 0:P], kT2[:, P:2 * P], ACT.Copy)
                    act.drain()
                    after(act, s["pe_kT"], t)
                    fn(kT2[:, P:2 * P], bank_S[:, 0:P], ACT.Copy).then_inc(s["kT_ev"], 1)
                if Dd:
                    after(act, s["lnm_ok"], t - 2)
                    fn(r[0:nd, :], r[0:nd, :], ACT.Identity, bias=lnm[0:nd, :], scale=lrs[0:nd, :]).then_inc(s["lz_ok"], 1)
                if B:
                    after(act, s["pe_uT"], t)
                    after(act, s["tail_ok"], t - 1)
                    fn(uT[:, :, TAPS - 1:], bank_S[:, 512:1024].rearrange("p (c t) -> p c t", c=CC),
                       ACT.Copy).then_inc(s["uT_ev"], 1)
                    if isinstance(t, int) and t == 0:
                        act.wait_ge(s["cw_ok"], 1)
                    act.drain()
                    after(act, s["pe_yN"], t - 1)
                    for c in range(CC):
                        last = fn(conv[:, c, :], uT[:, c, 0:P], ACT.Identity, bias=cw[:, c, TAPS:TAPS + 1], scale=cw[:, c, 0:1])
                    last.then_inc(s["conv0_ok"], 1)
                if Dd:
                    after(act, s["pe_hT"], t - 2)
                    after(act, s["pe_router"], t - 3)
                    fn(hT[:, :, 0:nd], T8[:, :, 0:nd], ACT.Copy).then_inc(s["hT_ev"], 1)
                if Cc:
                    after(act, s["cnm_ok"], t - 1)
                    after(act, s["pe_zT"], t - 2)
                    fn(z[0:nc_, :], M1[0:nc_, :], ACT.Identity, bias=cnm[0:nc_, :], scale=crs[0:nc_, :]).then_inc(s["z_ev"], 1)
                if B:
                    exps(smA, 0, s["nmA_ok"], s["expA_ok"], t)
                    products(t, 0)
                    after(act, s["pe_ptA"], t)
                    after(act, s["pe_pvA"], t - 1)
                    fn(ptA.rearrange("p h w t -> p (h w t)"), bank_T[:, :], ACT.Copy).then_inc(s["ptA_ev"], 1)
                if Dd:
                    after(act, s["ro_nm"], t - 2)
                    fn(eg4[0:nd, :], lg8[0:nd, 0:NG], ACT.Exp, bias=ngm[0:nd, :], scale=1.0,
                       accum_out=gsum[0:nd, :]).then_inc(s["ro_e1"], 1)
                    after(act, s["ro_d"], t - 2)
                    fn(re2[0:nd, :], rd[0:nd, :], ACT.Exp).then_inc(s["ro_e2"], 1)
                if B:
                    exps(smB, G, s["nmB_ok"], s["expB_ok"], t)
                    after(act, s["l_ok"], t)
                    after(act, s["pv_ev"], t - 1)
                    fn(es, dd, ACT.Exp).then_inc(s["es_ok"], 1)
                if Cc:
                    after(act, s["zlin_ok"], t - 1)
                    after(act, s["mixc_ok"], t - 2)
                    fn(zsig[:, :, 0:nc_], zlin[:, :, 0:nc_], ACT.Sigmoid).then_inc(s["zsig_ok"], 1)
                if B:
                    products(t, 1)
                if A:
                    after(act, s["incg_ev"], t + 1)
                    fn(cg[0:na, :], cg[0:na, :], ACT.Sigmoid).then_inc(s["glu_sig"], 1)
                if B:
                    after(act, s["pe_ptB"], t)
                    after(act, s["pe_pvB"], t - 1)
                    fn(ptB.rearrange("p h w t -> p (h w t)"), bank_T[:, :], ACT.Copy).then_inc(s["ptB_ev"], 1)
                    products(t, 2)
                    after(act, s["li_ok"], t)
                    after(act, s["pe_pvB"], t)
                    after(act, s["pe_atT"], t - 1)
                    for h in range(HEADS):
                        kv, gg = divmod(h, G)
                        last = fn(attn[:, (gg * KVH + kv) * HD:(gg * KVH + kv + 1) * HD], M0[:, h * HD:(h + 1) * HD],
                                  ACT.Copy, scale=li[:, h:h + 1])
                    last.then_inc(s["pv_ev"], 1)
                    after(act, s["pe_atT"], t)
                    after(act, s["pe_out1"], t - 1)
                    fn(mixT[:, 0:G, :].rearrange("p g t -> p (g t)"), M1[:, :], ACT.Copy).then_inc(s["atT_ev"], 1)

            def sample():
                act.wait_ge(s["fill_out"], 16 * fills)
                act.wait_ge(s["y_out2"], 16)
                after(act, s["prod_used"], NT * BATCHES - 1)
                act.wait_ge(s["pe_sA"], 1)
                fn(KsT.rearrange("p b s -> p (b s)"), bank_T[:, :], ACT.Copy)
                fn(qTs.rearrange("p g b -> p (g b)"), M0[:, 0:32], ACT.Copy)
                for c in range(CC):
                    at = (c // 2) * 512 + (c % 2) * 2 * NROW
                    fn(ext[:, c, :, 0:TAPS - 1], bank_S[:, at:at + 2 * NROW].rearrange("p (b j) -> p b j", b=DEC), ACT.Copy)
                    last = fn(ext[:, c, :, TAPS - 1], M0[:, 64 + c * DEC:64 + (c + 1) * DEC], ACT.Copy)
                last.then_inc(s["sA_ev"], 1)
                act.wait_ge(s["pe_sB"], 1)
                sT4 = view(sT, b=DEC, kv=KVH, g=G)
                for kv, bank in enumerate((M1, bank_S)):
                    last = fn(sT4[:, :, kv, :], view(bank[:, 0:DEC * G], b=DEC, g=G), ACT.Copy)
                last.then_inc(s["sB_ev"], 1)
                act.wait_ge(s["sm_ok"], 1)
                fn(Ps, M0[0:64, 128:256], ACT.Exp, bias=s_nm, scale=SCALE, accum_out=s_rs)
                fn(s_es, s_dd, ACT.Exp).then_inc(s["s_exp"], 1)
                act.wait_ge(s["pe_sD"], 1)
                fn(PTs, M1[:, 128:192], ACT.Copy).then_inc(s["sD_ev"], 1)
                act.wait_ge(s["pe_sF"], 1)
                o_v = M0[:, 256:256 + 64].rearrange("p (b kv g) -> p kv g b", b=DEC, kv=KVH)
                fn(mix_s[0:HD], o_v[0:HD, 0], ACT.Copy)
                fn(mix_s[HD:P], o_v[HD:P, 1], ACT.Copy).then_inc(s["s_fin"], 1)

            pipeline(act, step, sample)

            act.wait_ge(s["tab_ok"], 1)
            n_blocks = act.value_load(nblk_i[0:1, :], min_val=PAIRS // P + 1, max_val=NB)

            def turned(b):
                after(act, s["pe_xg"], b)
                after(act, s["pe_up"], b - 1)
                fn(xgT.rearrange("p k t -> p (k t)"), bank_T[:, :], ACT.Copy).then_inc(s["xgT_ev"], 1)

            def gated(b, j):
                after(act, s["pe_up"], b)
                after(act, s["g_ok"], b - 1)
                fn(sg, UP[j][:, 0:FF], ACT.Sigmoid).then_inc(s["a_sig"], 1)

            def result(b, j, i):
                after(act, s["pe_dn"], b + 1)
                after(act, s[f"y_out{j}"], i - 1 + (j == 2), per=16)
                dst = ye[:, j * D:j * D + 512]
                fn(dst, bank_S[:, 0:512], ACT.Copy, scale=table_g[:, bass.ds(b, 1)]).then_inc(s["y_ev0"], 1)
                after(act, s["y_ev0"], b)
                after(act, s["y_ev1"], b)
                act.dma_start(y_dram[bass.ds(b * P, P), :], ye[:, j * D:(j + 1) * D]).then_inc(s[f"y_out{j}"], 16)

            turned(0)
            for b in range(RING):
                gated(b, b)
                turned(b + 1)
                if b:
                    result(b - 1, b - 1, 0)
            with act.Fori(1, NB // RING) as i:
                for j in range(RING):
                    b = i * RING + j
                    with act.If(b < n_blocks):
                        gated(b, j)
                    with act.If(b + 1 < n_blocks):
                        turned(b + 1)
                    with act.If(b - 1 < n_blocks):
                        result(b - 1, (j - 1) % RING, i if j else i - 1)
            with act.If(NB - 1 < n_blocks):
                result(NB - 1, RING - 1, NB // RING - 1)

            def normal(t, q, n):
                act.wait_ge(s["c_nm"], t + 1)
                zz = cy[q][1][0:n, :]
                fn(zz, zz, ACT.Identity, bias=c_nmr[q][0:n, :], scale=c_rstd[q][0:n, :]).then_inc(s["c_z"], 1)

            with act.Fori(0, NT // SETS) as i:
                for q in range(SETS):
                    normal(i * SETS + q, q, P)
            normal(NT, 0, DEC)

        @block.vector
        def _(v):
            tt, ts, stt = nc.vector.tensor_tensor, nc.vector.tensor_scalar, nc.vector.scalar_tensor_tensor
            cp, ttr = nc.vector.tensor_copy, nc.vector.tensor_tensor_reduce

            v.wait_ge(s["const_in"], 16)
            v.memset(lg8, NEG)
            v.memset(counts[:, :], 0.0)
            v.memset(expert[:, :], 0.0)
            v.memset(gate[:, :], 0.0)
            v.memset(rank[:, :], 0.0)
            v.wait_ge(s["pe_cwT"], 1)
            cp(cw.rearrange("p c j -> p (c j)"), M1[:, 0:CC * (TAPS + 3)]).then_inc(s["cw_ok"], 1)
            v.drain()

            def softmax_max(kv, smx, sem_pe, sem_ev, sem_nm, t, flipped):
                after(v, sem_pe, t)
                after(v, flipped, t - 1)
                cp(carry, nsink[:, 0:1])
                v.drain()
                mask = C["band0"] if isinstance(t, int) and t == 0 else C["band"]
                c0 = kv * G
                for g in range(G):
                    last = ttr(smx[:, g, :], bank_S[:, g * 2 * P:(g + 1) * 2 * P], mask, 1.0, 3 * NEG, ALU.add, ALU.max,
                               mx[:, c0 + g:c0 + g + 1])
                last.then_inc(sem_ev, 1)
                v.drain()
                stt(nm[:, c0:c0 + G], mx[:, c0:c0 + G], -SCALE, nsink[:, c0:c0 + G], ALU.mult, ALU.min).then_inc(sem_nm, 1)

            def taps(t, j0, j1):
                for j in range(j0, j1):
                    for c in range(CC):
                        last = stt(conv[:, c, :], uT[:, c, j:j + P], cw[:, c, j:j + 1], conv[:, c, :], ALU.mult, ALU.add)
                    if j < TAPS - 1:
                        v.drain()
                return last

            def add_products(t, n):
                after(v, s["prod_ok"], t * BATCHES + n)
                for b in range(BATCH):
                    last = tt(conv, conv, prods[:, b], ALU.add)
                    if b < BATCH - 1:
                        v.drain()
                last.then_inc(s["prod_used"], 1)
                v.drain()

            def finish_conv(t):
                taps(t, TAIL, TAPS).then_inc(s["conv_ok"], 1)
                cp(tail, uT[:, :, P:P + TAPS - 1])
                v.drain()
                cp(uT[:, :, 0:TAPS - 1], tail).then_inc(s["tail_ok"], 1)

            def step(t):
                A, B, Cc, Dd = has(t + 1), has(t, NT - 1), has(t - 1), has(t - 2)
                na, nc_, nd = rows_of(t + 1), rows_of(t - 1), rows_of(t - 2)
                if isinstance(t, int) and t == 0:
                    v.wait_ge(s["init_ok"], 16 * 5)
                    v.wait_ge(s["s_sinks"], 16 * (1 + DEC))
                    ts(nsink[:, :], nsink[:, :], -1.0, None, ALU.mult)
                    ts(s_ns, s_ns, -1.0, None, ALU.mult)
                    v.drain()
                if has(t - 1, NT - 2):
                    finish_conv(t - 1)
                if Dd:
                    after(v, s["lz_ok"], t - 2)
                    tt(r[0:nd, :], r[0:nd, :], ln_g[0:nd, :], ALU.mult).then_inc(s["lg_ok"], 1)
                if A:
                    after(v, s["pe_inq"], t + 1)
                    tt(qk[0:na, 0:AD], P0[0:na, :], b_in[0:na, 0:AD], ALU.add).then_inc(s["inq_ev"], 1)
                if Cc:
                    after(v, s["pe_yN"], t - 1)
                    after(v, s["z_ev"], t - 2)
                    nc.vector.bn_stats(cst6[0:nc_, :], M1[0:nc_, :])
                    v.drain()
                    nc.vector.bn_aggr(cmv[0:nc_, :], cst6[0:nc_, :]).then_inc(s["cstat_ok"], 1)
                if B:
                    softmax_max(0, smA, s["pe_scA"], s["scA_ev"], s["nmA_ok"], t, s["pe_ptA"])
                    after(v, s["conv0_ok"], t)
                    taps(t, 1 + BATCH * BATCHES, 15)
                if A:
                    after(v, s["pe_inkv"], t + 1)
                    tt(qk[0:na, AD:], P1[0:na, 0:KVD], b_in[0:na, AD:AD + KVD], ALU.add)
                    after(v, s["v_ok"], t, NT - 1)
                    if isinstance(t, int) and t == NT - 1:
                        v.wait_ge(s["v_out"], 16)
                    tt(v_next[0:na, :], P1[0:na, KVD:2 * KVD], b_in[0:na, AD + KVD:AD + 2 * KVD],
                       ALU.add).then_inc(s["inkv_ev"], 1)
                    v.drain()
                    cs = C["rope"][0:na, bass.ds((t + 1) * 2 * HALF, 2 * HALF)].rearrange("p (w i) -> p w i", w=2)
                    hh = (HEADS + KVH) * 2
                    qv = qk[0:na, :].rearrange("p (h i) -> p h i", i=HALF)
                    rc = rot_c[0:na, :].rearrange("p (h i) -> p h i", i=HALF)
                    rsn = rot_s[0:na, :].rearrange("p (h i) -> p h i", i=HALF)
                    tt(rc, qv, cs[:, 0:1, :].broadcast_to([na, hh, HALF]), ALU.mult)
                    tt(rsn, qv, cs[:, 1:2, :].broadcast_to([na, hh, HALF]), ALU.mult)
                    v.drain()
                    after(v, s["pe_qT"], t, NT - 1)
                    after(v, s["pe_kT"], t, NT - 1)
                    if isinstance(t, int) and t == NT - 1:
                        v.wait_ge(s["k_out"], 16)
                    c4 = rot_c[0:na, :].rearrange("p (h w i) -> p h w i", w=2, i=HALF)
                    s4 = rot_s[0:na, :].rearrange("p (h w i) -> p h w i", w=2, i=HALF)
                    q5 = q_r[0:na, :].rearrange("p (g kv w i) -> p kv g w i", g=G, kv=KVH, w=2)
                    k4 = k_r[0:na, :].rearrange("p (kv w i) -> p kv w i", kv=KVH, w=2)
                    for w, op in ((0, ALU.subtract), (1, ALU.add)):
                        for kv in range(KVH):
                            hs = slice(kv * G, (kv + 1) * G)
                            last = tt(q5[:, kv, :, w, :], c4[:, hs, w, :], s4[:, hs, 1 - w, :], op)
                    last.then_inc(s["rope_q"], 1)
                    for w, op in ((0, ALU.subtract), (1, ALU.add)):
                        last = tt(k4[:, :, w, :], c4[:, HEADS:, w, :], s4[:, HEADS:, 1 - w, :], op)
                    last.then_inc(s["rope_k"], 1)
                if Dd:
                    after(v, s["pe_router"], t - 2)
                    after(v, s["ro_e1"], t - 3)
                    cp(lg8[0:nd, 0:NG], M0[0:nd, 0:NG])
                    cp(le[0:nd, :], M0[0:nd, NG:NG + NE]).then_inc(s["ro_ev"], 1)
                    v.drain()
                    nc.vector.max(g8[0:nd, :], lg8[0:nd, :])
                    v.drain()
                    nc.vector.max_index(gi_u[0:nd, :], g8[0:nd, :], lg8[0:nd, :])
                    ts(ngm[0:nd, :], g8[0:nd, 0:1], -1.0, None, ALU.mult).then_inc(s["ro_nm"], 1)
                    v.drain()
                    cp(gidx[0:nd, :], gi_u[0:nd, 0:1])
                    v.drain()
                    ts(pen[0:nd, :], C["iota"][0:nd, 0:NG], gidx[0:nd, :], NEG, ALU.not_equal, ALU.mult)
                    v.drain()
                    le3 = le[0:nd, :].rearrange("p (g e) -> p g e", g=NG)
                    tt(le3, le3, pen[0:nd, :].unsqueeze(2).broadcast_to([nd, NG, EPG]), ALU.add)
                    v.drain()
                    nc.vector.max(v8[0:nd, :], le[0:nd, :])
                    v.drain()
                    nc.vector.max_index(ei_u[0:nd, :], v8[0:nd, :], le[0:nd, :])
                    tt(rd[0:nd, :], v8[0:nd, 1:2], v8[0:nd, 0:1], ALU.subtract).then_inc(s["ro_d"], 1)
                    v.drain()
                    cp(e2s[0:nd, :], ei_u[0:nd, 0:2])
                    if not B:
                        v.drain()
                if Cc:
                    after(v, s["pe_zT"], t - 1)
                    for c in range(CC):
                        last = ts(zlin[:, c, 0:nc_], M1[:, c * P:c * P + nc_], cw[:, c, TAPS + 1:TAPS + 2],
                                  cw[:, c, TAPS + 2:TAPS + 3], ALU.mult, ALU.add)
                    last.then_inc(s["zlin_ok"], 1)
                if B:
                    add_products(t, 0)
                if B:
                    softmax_max(1, smB, s["pe_scB"], s["scB_ev"], s["nmB_ok"], t, s["pe_ptB"])
                    v.drain()
                    tt(dd, nm, nsink[:, :], ALU.subtract).then_inc(s["l_ok"], 1)
                if A:
                    after(v, s["pe_inca"], t + 1)
                    tt(ca[0:na, :], P0[0:na, :], b_in[0:na, AD + 2 * KVD:AD + 2 * KVD + CH], ALU.add).then_inc(s["inca_ev"], 1)
                if Dd:
                    after(v, s["ro_e1"], t - 2)
                    after(v, s["ro_e2"], t - 2)
                    stt(rr[0:nd, :], re2[0:nd, :], 1.0, gsum[0:nd, :], ALU.add, ALU.mult)
                    ts(oh1[0:nd, :], C["iota"][0:nd, 0:NE], e2s[0:nd, 0:1], None, ALU.is_equal)
                    ts(oh2[0:nd, :], C["iota"][0:nd, 0:NE], e2s[0:nd, 1:2], None, ALU.is_equal)
                    v.drain()
                    nc.vector.reciprocal(g2s[0:nd, 0:1], rr[0:nd, :])
                    tt(ohs[0:nd, :], oh1[0:nd, :], oh2[0:nd, :], ALU.add).then_inc(s["onehot_ok"], 1)
                    v.drain()
                    tt(g2s[0:nd, 1:2], g2s[0:nd, 0:1], re2[0:nd, :], ALU.mult)
                    v.drain()
                    cp(gate[0:nd, bass.ds((t - 2) * 2, 2)], g2s[0:nd, :])
                    cp(expert[0:nd, bass.ds((t - 2) * 2, 2)], e2s[0:nd, :])
                if B:
                    taps(t, 15, 18)
                if Cc:
                    after(v, s["zsig_ok"], t - 1)
                    after(v, s["pe_out1"], t - 2)
                    tt(mixT[:, G:KD, 0:nc_], zlin[:, :, 0:nc_], zsig[:, :, 0:nc_], ALU.mult).then_inc(s["mixc_ok"], 1)
                if A:
                    after(v, s["pe_incg"], t + 1)
                    tt(cg[0:na, :], P1[0:na, :], b_in[0:na, AD + 2 * KVD + CH:], ALU.add).then_inc(s["incg_ev"], 1)
                if Dd:
                    after(v, s["pe_rank"], t - 2)
                    tt(rk[0:nd, :], M0[0:nd, 0:NE], counts[0:nd, :], ALU.add)
                    v.drain()
                    tt(counts[:, :], counts[:, :], M0[:, NE:2 * NE], ALU.add).then_inc(s["rk_ev"], 1)
                    ttr(ttr_out[0:nd, :], oh1[0:nd, :], rk[0:nd, :], 1.0, 0.0, ALU.mult, ALU.add, r2s[0:nd, 0:1])
                    v.drain()
                    ttr(ttr_out[0:nd, :], oh2[0:nd, :], rk[0:nd, :], 1.0, 0.0, ALU.mult, ALU.add, r2s[0:nd, 1:2])
                    v.drain()
                    cp(rank[0:nd, bass.ds((t - 2) * 2, 2)], r2s[0:nd, :])
                if B:
                    add_products(t, 1)
                    taps(t, 18, 20)
                if A:
                    after(v, s["glu_sig"], t + 1)
                    after(v, s["pe_uT"], t, NT - 1)
                    if isinstance(t, int) and t == NT - 1:
                        v.wait_ge(s["u_out"], 16)
                    tt(u[0:na, :], ca[0:na, :], cg[0:na, :], ALU.mult).then_inc(s["u_ok"], 1)
                if B:
                    taps(t, 20, 22)
                    add_products(t, 2)
                    taps(t, 22, TAIL)
                if B:
                    after(v, s["es_ok"], t)
                    after(v, s["pv_ev"], t - 1)
                    tt(li, rs, es, ALU.add)
                    v.drain()
                    nc.vector.reciprocal(li, li).then_inc(s["li_ok"], 1)
                if Cc:
                    after(v, s["xres_ok"], t - 1)
                    after(v, s["pe_hT"], t - 2)
                    if has(t - 2):
                        v.wait_ge(s["h_out"], (t - 1) * 16)
                    after(v, s["pe_out0"], t - 1)
                    tt(r[0:nc_, 0:512], P0[0:nc_, :], xres[0:nc_, 0:512], ALU.add).then_inc(s["out0_ev"], 1)
                if Cc:
                    after(v, s["pe_out1"], t - 1)
                    tt(r[0:nc_, 512:], P1[0:nc_, :], xres[0:nc_, 512:], ALU.add).then_inc(s["out1_ev"], 1)
                    v.drain()
                    for i in range(2):
                        last = nc.vector.bn_stats(lst[0:nc_, 6 * i:6 * i + 6], r[0:nc_, 512 * i:512 * (i + 1)])
                    last.then_inc(s["r_ok"], 1)
                    v.drain()
                    nc.vector.bn_aggr(lmv[0:nc_, :], lst[0:nc_, :]).then_inc(s["lstat_ok"], 1)

            def sample():
                finish_conv(NT - 1)
                v.wait_ge(s["sA_ev"], 1)
                after(v, s["pe_xT"], NT)
                for c in range(CC):
                    tt(prod[:, c], ext[:, c], cw[:, c:c + 1, 0:TAPS].broadcast_to([P, DEC, TAPS]), ALU.mult)
                v.drain()
                for c in range(CC):
                    nc.vector.tensor_reduce(conv_s[:, c, :], prod[:, c], AX, ALU.add)
                v.drain()
                for c in range(CC):
                    last = ts(conv_s[:, c, :], conv_s[:, c, :], cw[:, c, TAPS:TAPS + 1], None, ALU.add)
                last.then_inc(s["conv_ok"], 1)
                v.wait_ge(s["pe_sC"], 1)
                nc.vector.tensor_reduce(s_mx, M0[0:64, 128:256], AX, ALU.max)
                v.drain()
                stt(s_nm, s_mx, -SCALE, s_ns, ALU.mult, ALU.min)
                v.drain()
                tt(s_dd, s_nm, s_ns, ALU.subtract).then_inc(s["sm_ok"], 1)
                v.wait_ge(s["s_exp"], 1)
                tt(s_li, s_rs, s_es, ALU.add)
                v.drain()
                nc.vector.reciprocal(s_li, s_li)
                v.drain()
                ts(Ps, Ps, s_li, None, ALU.mult).then_inc(s["s_p"], 1)

            pipeline(v, step, sample)

            after(v, s["h_ok"], NT)
            v.wait_ge(s["h_out"], 16 * (NT + 1))
            v.drain()
            tt(cmpb.rearrange("p (e m) -> p e m", e=NE), counts[:, :].unsqueeze(2).broadcast_to([P, NE, MAXC]),
               C["thresh"].unsqueeze(1).broadcast_to([P, NE, MAXC]), ALU.is_gt)
            oh3 = oh34.rearrange("p (q e) -> p q e", e=NE)
            nq = 2 * (NT + 1)
            tt(oh3, expert[:, :].unsqueeze(2).broadcast_to([P, nq, NE]),
               C["iota"][:, 0:NE].unsqueeze(1).broadcast_to([P, nq, NE]), ALU.is_equal)
            v.drain()
            nc.vector.tensor_reduce(nblk, cmpb.rearrange("p (e m) -> p e m", e=NE), AX, ALU.add)
            v.drain()
            nc.vector.tensor_tensor_scan(cum, C["ones"][:, 0:NE], nblk, 0.0, ALU.mult, ALU.add)
            v.drain()
            tt(startb, cum, nblk, ALU.subtract)
            cp(nblk_i[0:1, :], cum[0:1, NE - 1:NE])
            v.drain()
            tt(oh3, oh3, startb.unsqueeze(1).broadcast_to([P, nq, NE]), ALU.mult)
            v.drain()
            nc.vector.tensor_reduce(st34, oh3, AX, ALU.add)
            v.drain()
            stt(slf, st34, float(P), rank[:, :], ALU.mult, ALU.add)
            v.drain()
            cp(slot_i[:, :], slf)
            v.drain()
            ts(lo_i[:, :], slot_i[:, :], P - 1, None, ALU.bitwise_and)
            ts(hi_i[:, :], slot_i[:, :], 7, None, ALU.arith_shift_right)
            v.drain()
            cp(lof, lo_i[:, :])
            cp(hif, hi_i[:, :])
            v.drain()
            for t in range(NT + 1):
                n = rows_of(t)
                after(v, s["pe_tab"], t - 2)
                for k in range(2):
                    q = 2 * t + k
                    b0 = ge[t % 2][0:n, k * 256:(k + 1) * 256]
                    ts(b0[:, 0:P], C["iota"][0:n, :], lof[0:n, q:q + 1], None, ALU.is_equal)
                    ts(b0[:, P:P + NBT], C["iota"][0:n, 0:NBT], hif[0:n, q:q + 1], C["tok"][0:n, t:t + 1], ALU.is_equal, ALU.mult)
                    last = ts(b0[:, P + NBT:P + 2 * NBT], C["iota"][0:n, 0:NBT], hif[0:n, q:q + 1], gate[0:n, q:q + 1],
                              ALU.is_equal, ALU.mult)
                last.then_inc(s["tab_build"], 1)
            v.wait_ge(s["pe_tab"], NT + 1)
            cp(table_i[:, :], M0[:, 0:NBT])
            cp(table_g, M0[:, NBT:2 * NBT]).then_inc(s["tab_ok"], 1)
            b3 = bexp.rearrange("p (b e) -> p b e", e=NE)
            s3 = bstep.rearrange("p (b e) -> p b e", e=NE)
            tt(b3[0:1], C["iota"][0:1, 0:NBT].unsqueeze(2).broadcast_to([1, NBT, NE]),
               cum[0:1, :].unsqueeze(1).broadcast_to([1, NBT, NE]), ALU.is_ge)
            ts(used_b[0:1, :], C["iota"][0:1, 0:NBT], cum[0:1, NE - 1:NE], None, ALU.is_lt)
            ts(cum_i[0:1, :], cum[0:1, :], 1.0, None, ALU.add)
            v.drain()
            nc.vector.tensor_reduce(bex[0:1, :], b3[0:1], AX, ALU.add)
            tt(s3[0:1], b3[0:1], C["slot_step"][0:1, :].unsqueeze(1).broadcast_to([1, NBT, NE]), ALU.mult)
            for j in range(RING):
                nc.vector.tensor_reduce(stores_f[0:1, j:j + 1], used_b[0:1, 0:NB].rearrange("p (i j) -> p j i", j=RING)[:, j], AX, ALU.add)
            v.drain()
            nc.vector.tensor_reduce(woff[0:1, :], s3[0:1], AX, ALU.add)
            ts(bex_i[0:1, 0:NBT], bex[0:1, :], 16.0, 16.0, ALU.mult, ALU.add)
            cp(stores_i[0:1, :], stores_f[0:1, :])
            v.drain()
            cp(woff_i[0:1, :], woff[0:1, :]).then_inc(s["eids_ok"], 1)
            v.drain()

            n_blocks = v.value_load(nblk_i[0:1, :], min_val=PAIRS // P + 1, max_val=NB)

            def swiglu(b, j):
                after(v, s["a_sig"], b)
                tt(gs, UP[j][:, 0:FF], sg, ALU.mult)
                v.drain()
                after(v, s["pe_gT"], b - 1)
                tt(gu, UP[j][:, FF:2 * FF], gs, ALU.mult).then_inc(s["g_ok"], 1)

            def turned(b):
                after(v, s["pe_gT"], b)
                after(v, s["pe_dn"], b)
                cp(gT.rearrange("p k t -> p (k t)"), M0[:, 0:FF]).then_inc(s["gT_ev"], 1)

            def result(b, j, i):
                after(v, s["pe_dn"], b + 1)
                after(v, s[f"y_out{j}"], i - 1 + (j == 2), per=16)
                ts(ye[:, j * D + 512:(j + 1) * D], bank_S[:, 512:], table_g[:, bass.ds(b, 1)], None,
                   ALU.mult).then_inc(s["y_ev1"], 1)

            for b in range(RING):
                if b:
                    turned(b - 1)
                swiglu(b, b)
                if b:
                    result(b - 1, b - 1, 0)
            with v.Fori(1, NB // RING) as i:
                for j in range(RING):
                    b = i * RING + j
                    with v.If(b - 1 < n_blocks):
                        turned(b - 1)
                    with v.If(b < n_blocks):
                        swiglu(b, j)
                    with v.If(b - 1 < n_blocks):
                        result(b - 1, (j - 1) % RING, i if j else i - 1)
            with v.If(NB - 1 < n_blocks):
                turned(NB - 1)
                result(NB - 1, RING - 1, NB // RING - 1)

            v.wait_ge(s["ln2_in"], 32)

            def combine(t, q, n, visit):
                v.wait_ge(s[f"c_g{q}"], 32 * (visit + 1))
                v.wait_ge(s[f"c_h{q}"], 16 * (visit + 1))
                y0, y1, hh = cy[q][0][0:n, :], cy[q][1][0:n, :], chh[q][0:n, :]
                tt(y0, y0, y1, ALU.add)
                v.drain()
                stt(y1, hh, ALPHA, y0, ALU.mult, ALU.add)
                v.drain()
                for i in range(2):
                    nc.vector.bn_stats(c_st[q][0:n, 6 * i:6 * i + 6], y1[:, 512 * i:512 * (i + 1)])
                v.drain()
                nc.vector.bn_aggr(c_mv[q][0:n, :], c_st[q][0:n, :]).then_inc(s["c_st"], 1)

            def finish(t, q, n):
                y1 = cy[q][1][0:n, :]
                v.wait_ge(s["c_z"], t + 1)
                tt(y1, y1, ln_g[0:n, :], ALU.mult)
                v.drain()
                tt(y1, y1, ln_b[0:n, :], ALU.add).then_inc(s["c_y"], 1)

            combine(0, 0, P, 0)
            with v.Fori(0, NT // SETS - 1) as i:
                for q in range(SETS):
                    combine(i * SETS + q + 1, (q + 1) % SETS, P, i + (q + 1) // SETS)
                    finish(i * SETS + q, q, P)
            for t in range(NT - SETS, NT + 1):
                if t < NT:
                    combine(t + 1, (t + 1) % SETS, rows_of(t + 1), (t + 1) // SETS)
                finish(t, t % SETS, rows_of(t))

        @block.gpsimd
        def _(g):
            gtt, gts, gcp = nc.gpsimd.tensor_tensor, nc.gpsimd.tensor_scalar, nc.gpsimd.tensor_copy

            g.memset(tick[:, :], 0.0)
            g.memset(V2[:, 1, :], 0.0)
            g.memset(zeros, 0.0)
            g.memset(uT[:, :, 0:TAPS - 1], 0.0)
            g.memset(kT2[:, P:2 * P], 0.0).then_inc(s["g_init"], 1)
            g.drain()

            col = [0]

            def hold_ge(sem, value):
                g.wait_ge(sem, value)
                if not isinstance(value, int):
                    if col[0] == 0:
                        gtt(tick[:, 1:2], tick[:, 0:1], tick[:, 0:1], ALU.add)
                        g.drain()
                    else:
                        col[0] += 1
                        gtt(tick[:, col[0]:col[0] + 1], tick[:, 0:1], tick[:, 0:1], ALU.add)

            def hold(sem, tile, last=None):
                if isinstance(tile, int):
                    after(g, sem, tile, last)
                else:
                    hold_ge(sem, tile + 1)

            def rstd(mv, ve, rstd_, nmr, n, sem):
                gts(ve[0:n, :], mv[0:n, 1:2], EPS, None, ALU.add)
                g.drain()
                gtt(rstd_[0:n, :], ve[0:n, :], C["mhalf"][0:n, :], ALU.pow)
                g.drain()
                gtt(ve[0:n, :], mv[0:n, 0:1], rstd_[0:n, :], ALU.mult)
                g.drain()
                gts(nmr[0:n, :], ve[0:n, :], -1.0, None, ALU.mult).then_inc(sem, 1)

            def step(t):
                B, Cc = has(t, NT - 1), has(t - 1)
                nc_ = rows_of(t - 1)
                if has(t - 2):
                    nd = rows_of(t - 2)
                    hold(s["lg_ok"], t - 2)
                    gtt(r[0:nd, :], r[0:nd, :], ln_b[0:nd, :], ALU.add).then_inc(s["h_ok"], 1)
                if Cc:
                    hold(s["cstat_ok"], t - 1)
                    hold(s["z_ev"], t - 2)
                    rstd(cmv, cve, crs, cnm, nc_, s["cnm_ok"])
                if B:
                    hold(s["pe_pvB"], t - 1)
                    gcp(V2[:, 0, :], V2[:, 1, :])
                    g.drain()
                    hold(s["inkv_ev"], t)
                    gcp(V2[:, 1, :], v_next).then_inc(s["v_ok"], 1)
                if Cc:
                    hold_ge(s["xres_in"], t * 16)
                    gts(xres[0:nc_, :], xres[0:nc_, :], ALPHA, None, ALU.mult)
                    g.drain()
                    gtt(xres[0:nc_, :], xres[0:nc_, :], b_out[0:nc_, :], ALU.add).then_inc(s["xres_ok"], 1)
                    hold(s["lstat_ok"], t - 1)
                    rstd(lmv, lve, lrs, lnm, nc_, s["lnm_ok"])

            pipeline(g, step, lambda: None)
            col[0] = 1

            hold_ge(s["tab_ok"], 1)
            hold_ge(s["h_out"], 16 * (NT + 1))
            n_blocks = g.value_load(nblk_i[0:1, :], min_val=PAIRS // P + 1, max_val=NB)

            def gather(b, j, i):
                hold(s["pe_xg"], b - RING)
                gcp(gidx3[:, j:j + 1], table_i[:, bass.ds(b, 1)]).then_inc(s["idx_ok"], 1)
                hold_ge(s["idx_ok"], b + 1)
                g.indirect_dma_start(xg[j], None, h_dram,
                                     bass.IndirectOffsetOnAxis(ap=gidx3[:, j:j + 1], axis=0)).then_inc(s[f"xg_in{j}"], 16)

            for b in range(RING):
                gather(b, b, 0)
            with g.Fori(1, NB // RING) as i:
                for j in range(RING):
                    with g.If(i * RING + j < n_blocks):
                        gather(i * RING + j, j, i)

            hold_ge(s["eids_ok"], 1)
            for j in range(RING):
                stores = g.value_load(stores_i[0:1, j:j + 1], min_val=PAIRS // P // RING, max_val=NB // RING)
                hold_ge(s[f"y_out{j}"], (stores + (j == 2)) * 16)

            def pick(t, q, visit):
                if not isinstance(visit, int) or visit:
                    hold_ge(s[f"c_o{q}"], visit * 16)
                gcp(cidx[:, 2 * q:2 * q + 2], slot_i[:, bass.ds(2 * t, 2)]).then_inc(s["i_c"], 1)
                hold_ge(s["i_c"], t + 1)
                for k in range(2):
                    g.indirect_dma_start(cy[q][k], None, y_dram,
                                         bass.IndirectOffsetOnAxis(ap=cidx[:, 2 * q + k:2 * q + k + 1], axis=0)
                                         ).then_inc(s[f"c_g{q}"], 16)

            def stats(t, q, n):
                hold_ge(s["c_st"], t + 1)
                gts(c_ve[q][0:n, :], c_mv[q][0:n, 1:2], EPS, None, ALU.add).then_inc(s["c_m"], 1)
                hold_ge(s["c_m"], 3 * t + 1)
                gtt(c_rstd[q][0:n, :], c_ve[q][0:n, :], C["mhalf"][0:n, :], ALU.pow).then_inc(s["c_m"], 1)
                hold_ge(s["c_m"], 3 * t + 2)
                gtt(c_ve[q][0:n, :], c_mv[q][0:n, 0:1], c_rstd[q][0:n, :], ALU.mult).then_inc(s["c_m"], 1)
                hold_ge(s["c_m"], 3 * t + 3)
                gts(c_nmr[q][0:n, :], c_ve[q][0:n, :], -1.0, None, ALU.mult).then_inc(s["c_nm"], 1)

            for m in range(3):
                g.wait_ge(s[f"w{m}_ld"], 16 * NE)
            for t in range(SETS - 1):
                pick(t, t, 0)
            stats(0, 0, P)
            pick(SETS - 1, SETS - 1, 0)
            with g.Fori(0, NT // SETS - 1) as i:
                for q in range(SETS):
                    stats(i * SETS + q + 1, (q + 1) % SETS, P)
                    pick((i + 1) * SETS + q, q, i + 1)
            for t in range(NT - SETS + 1, NT + 1):
                stats(t, t % SETS, rows_of(t))
                if t + SETS - 1 == NT:
                    pick(NT, 0, NT // SETS)


INS = {
    "x_prompt": (SEQ, D), "x_sample": (DEC, D), "cache_k": (DEC, WIN, KVD), "cache_v": (DEC, WIN, KVD),
    "state_conv": (DEC, TAPS - 1, CH), "w_in": (D, IN), "b_in": (1, IN), "sinks": (1, HEADS),
    "conv_w": (TAPS, CH), "conv_b": (1, CH), "ln_conv_g": (1, CH), "ln_conv_b": (1, CH), "w_out": (D, D),
    "b_out": (1, D), "ln1_g": (1, D), "ln1_b": (1, D), "w_router_group": (D, NG), "w_router_expert": (D, NE),
    "w1": (NE, D, FF), "w3": (NE, D, FF), "w2": (NE, FF, D), "ln2_g": (1, D), "ln2_b": (1, D),
}
OUTS = {
    "y_prompt": ((SEQ, D), (1, SEQ, D)), "y_sample": ((DEC, D), (DEC, 1, D)),
    "new_k_prompt": ((WIN, KVD), (1, 1, WIN, KVH, HD)), "new_v_prompt": ((WIN, KVD), (1, 1, WIN, KVH, HD)),
    "new_conv_prompt": ((TAPS - 1, CH), (1, 1, TAPS - 1, CH)),
    "new_k_sample": ((DEC, WIN, KVD), (1, DEC, WIN, KVH, HD)),
    "new_v_sample": ((DEC, WIN, KVD), (1, DEC, WIN, KVH, HD)),
    "new_conv_sample": ((DEC, TAPS - 1, CH), (1, DEC, TAPS - 1, CH)),
}


def kernel(**inputs):
    import concourse.bacc as bacc
    from concourse.bass_utils import run_bass_kernel_spmd

    nc = bacc.Bacc("TRN2", target_bir_lowering=False, num_devices=1)
    arrays, a = {}, {}
    for name, shape in INS.items():
        arrays[f"in_{name}"] = np.ascontiguousarray(inputs[name]).reshape(shape)
    arrays["in_consts"] = constants()
    for name, value in arrays.items():
        a[name[3:]] = nc.dram_tensor(name, value.shape, F32, kind="ExternalInput").ap()
    o = {name: nc.dram_tensor(f"out_{name}", flat, F32, kind="ExternalOutput").ap()
         for name, (flat, _) in OUTS.items()}
    h_dram = nc.dram_tensor("h_rows", (TOK, D), F32, kind="Internal").ap()
    y_dram = nc.dram_tensor("expert_rows", (NB * P, D), F32, kind="Internal").ap()
    layer(nc, a, o, (h_dram, y_dram))
    got = run_bass_kernel_spmd(nc, [arrays], core_ids=[0]).results[0]
    return tuple(got[f"out_{name}"].reshape(shape) for name, (_, shape) in OUTS.items())
```
